# Optimizing a Trainium2 kernel written in Bass

```python
import jax
import jax.numpy as jnp
from jax import lax
import numpy as np

D_MODEL = 2048
BATCH = 1
SEQ = 512
DEPTH = 1
DEC_BATCH = 8
DEC_SEQ = 4
PAST_LEN = 2048
PAGE_SIZE = 128

D_MIX = D_MODEL
N_GROUPS = 4
D_GROUP = D_MIX // N_GROUPS
HEAD_DIM = 64
N_HEADS_FOX = D_GROUP // HEAD_DIM
N_HEADS_SB = D_GROUP // HEAD_DIM
POOL_WINDOWS = (2, 4, 8, 16)
POOL_MAX = max(POOL_WINDOWS)
POOL_CH = D_GROUP // len(POOL_WINDOWS)
CONV_W = 4
LRU_BLOCKS = 8
LRU_BLOCK_DIM = D_GROUP // LRU_BLOCKS
LRU_C = 8.0
D_FF = 4 * D_MODEL
D_IN = 9 * D_GROUP + N_HEADS_FOX
QBLOCK = 128
FORGET_BIAS = 2.0
EPS = 1e-6

kernel_name = 'hybrid_pool_rglru_fox_stickbreak_step'

def rms_norm(x, g):
    xf = x.astype(jnp.float32)
    y = xf * lax.rsqrt(jnp.mean(xf * xf, axis=-1, keepdims=True) + EPS)
    return (y * g.astype(jnp.float32)).astype(x.dtype)

def gather_pages(pool, page_table):
    rows = pool[page_table]
    return rows.reshape((rows.shape[0], rows.shape[1] * rows.shape[2]) + rows.shape[3:])

def sweep_queries(fn, q_arrays, q_pos):
    t = q_pos.shape[0]
    if t <= QBLOCK:
        return fn(*q_arrays, q_pos)
    nb = t // QBLOCK
    blocks = tuple(a.reshape((a.shape[0], nb, QBLOCK) + a.shape[2:]).swapaxes(0, 1) for a in q_arrays)
    out = lax.map(lambda args: fn(*args), blocks + (q_pos.reshape(nb, QBLOCK),))
    out = out.swapaxes(0, 1)
    return out.reshape((out.shape[0], t) + out.shape[3:])

def pool_mixer(u, prev, pos0, pool_w, pool_scale):
    b, t, c = u.shape
    p = POOL_MAX - 1
    ext = jnp.concatenate([prev.astype(jnp.float32), u.astype(jnp.float32)], axis=1)
    cs = jnp.concatenate([jnp.zeros((b, 1, c), jnp.float32), jnp.cumsum(ext, axis=1)], axis=1)
    end = cs[:, p + 1:p + 1 + t]
    pos = pos0 + jnp.arange(t)
    means = []
    for g, w in enumerate(POOL_WINDOWS):
        lo, hi = g * POOL_CH, (g + 1) * POOL_CH
        start = cs[:, p + 1 - w:p + 1 - w + t, lo:hi]
        cnt = jnp.minimum(w, pos + 1).astype(jnp.float32)[None, :, None]
        means.append((end[..., lo:hi] - start) / cnt)
    d = jnp.concatenate(means, axis=-1) - ext[:, p:]
    d = d.reshape(b, t, len(POOL_WINDOWS), POOL_CH).astype(u.dtype)
    y = jnp.einsum('btgc,gcd->btgd', d, pool_w).reshape(b, t, c) * pool_scale
    return y, ext[:, -p:].astype(u.dtype)

def rglru_mixer(xb, gate, conv_prev, h0, pos0, conv_w, conv_b, wa, ba, wx, bx, lam):
    b, t, c = xb.shape
    ext = jnp.concatenate([conv_prev.astype(xb.dtype), xb], axis=1)
    xc = conv_b + sum(ext[:, k:k + t] * conv_w[k] for k in range(CONV_W))
    xblk = xc.reshape(b, t, LRU_BLOCKS, LRU_BLOCK_DIM)
    r = jax.nn.sigmoid(jnp.einsum('btnd,nde->btne', xblk, wa).reshape(b, t, c) + ba)
    i = jax.nn.sigmoid(jnp.einsum('btnd,nde->btne', xblk, wx).reshape(b, t, c) + bx)
    log_a = -LRU_C * r.astype(jnp.float32) * jax.nn.softplus(-lam.astype(jnp.float32))
    mult = jnp.sqrt(-jnp.expm1(2.0 * log_a))
    pos = pos0 + jnp.arange(t)
    mult = jnp.where((pos == 0)[None, :, None], 1.0, mult)
    a = jnp.exp(log_a)
    u = mult * (i * xc).astype(jnp.float32)

    def step(h, au):
        h = au[0] * h + au[1]
        return h, h

    h_last, hs = lax.scan(step, h0.astype(jnp.float32), (a.swapaxes(0, 1), u.swapaxes(0, 1)))
    y = jax.nn.gelu(gate) * hs.swapaxes(0, 1).astype(xb.dtype)
    return y, ext[:, -(CONV_W - 1):], h_last.astype(xb.dtype)

def fox_block(q, cq, qpos, k, v, ck_t, kpos):
    s = jnp.einsum('bqhd,bkhd->bhqk', q, k).astype(jnp.float32) * (HEAD_DIM ** -0.5)
    s = s + cq.astype(jnp.float32).transpose(0, 2, 1)[..., None] - ck_t[:, :, None, :]
    s = jnp.where((kpos[None, :] <= qpos[:, None])[None, None], s, -jnp.inf)
    p = jax.nn.softmax(s, axis=-1)
    return jnp.einsum('bhqk,bkhd->bqhd', p.astype(v.dtype), v)

def sb_block(q, qpos, k, v, kpos):
    z = jnp.einsum('bqhd,bkhd->bhqk', q, k).astype(jnp.float32) * (HEAD_DIM ** -0.5)
    mask = (kpos[None, :] < qpos[:, None])[None, None]
    log_1m = jnp.where(mask, jax.nn.log_sigmoid(-z), 0.0)
    rest = lax.cumsum(log_1m, axis=3, reverse=True) - log_1m
    wgt = jnp.where(mask, jnp.exp(jax.nn.log_sigmoid(z) + rest), 0.0)
    return jnp.einsum('bhqk,bkhd->bqhd', wgt.astype(v.dtype), v)

def token_mixers(h, pool_prev, conv_prev, lru_h0, past, w_in, pool_w, pool_scale, conv_w, conv_b,
                 lru_wa, lru_ba, lru_wx, lru_bx, lru_lambda, fox_bf, fox_q_g, fox_k_g, out_g, w_out):
    b, t, _ = h.shape
    G = D_GROUP
    proj = jnp.einsum('btd,de->bte', h, w_in)

    def heads(lo, n):
        return proj[..., lo:lo + n * HEAD_DIM].reshape(b, t, n, HEAD_DIM)

    u_pool = proj[..., 0:G]
    x_lru = proj[..., G:2 * G]
    g_lru = proj[..., 2 * G:3 * G]
    fq = rms_norm(heads(3 * G, N_HEADS_FOX), fox_q_g)
    fk = rms_norm(heads(4 * G, N_HEADS_FOX), fox_k_g)
    fv = heads(5 * G, N_HEADS_FOX)
    f_logit = proj[..., 6 * G:6 * G + N_HEADS_FOX]
    off = 6 * G + N_HEADS_FOX
    sq = heads(off, N_HEADS_SB)
    sk = heads(off + G, N_HEADS_SB)
    sv = heads(off + 2 * G, N_HEADS_SB)
    logf = jax.nn.log_sigmoid((f_logit + fox_bf).astype(jnp.float32)).astype(h.dtype)

    if past is None:
        p_len = 0
        fk_all, fv_all, logf_all, sk_all, sv_all = fk, fv, logf, sk, sv
    else:
        past_fox_kv, past_logf, past_sb_kv = past
        p_len = past_logf.shape[1]
        fk_all = jnp.concatenate([past_fox_kv[:, :, 0].astype(h.dtype), fk], axis=1)
        fv_all = jnp.concatenate([past_fox_kv[:, :, 1].astype(h.dtype), fv], axis=1)
        logf_all = jnp.concatenate([past_logf.astype(h.dtype), logf], axis=1)
        sk_all = jnp.concatenate([past_sb_kv[:, :, 0].astype(h.dtype), sk], axis=1)
        sv_all = jnp.concatenate([past_sb_kv[:, :, 1].astype(h.dtype), sv], axis=1)
    qpos = p_len + jnp.arange(t)
    kpos = jnp.arange(p_len + t)

    c_all = jnp.cumsum(logf_all.astype(jnp.float32), axis=1)
    cq = c_all[:, p_len:]
    ck_t = c_all.transpose(0, 2, 1)
    y_fox = sweep_queries(lambda qb, cqb, pb: fox_block(qb, cqb, pb, fk_all, fv_all, ck_t, kpos), (fq, cq), qpos)
    y_sb = sweep_queries(lambda qb, pb: sb_block(qb, pb, sk_all, sv_all, kpos), (sq,), qpos)

    y_pool, pool_new = pool_mixer(u_pool, pool_prev, p_len, pool_w, pool_scale)
    y_lru, conv_new, lru_new = rglru_mixer(x_lru, g_lru, conv_prev, lru_h0, p_len, conv_w, conv_b,
                                           lru_wa, lru_ba, lru_wx, lru_bx, lru_lambda)

    y_cat = jnp.stack([y_pool, y_lru, y_fox.reshape(b, t, G), y_sb.reshape(b, t, G)], axis=2)
    y_cat = rms_norm(y_cat, out_g.reshape(N_GROUPS, G)).reshape(b, t, D_MIX)
    y = jnp.einsum('btc,cd->btd', y_cat, w_out)
    new_state = (jnp.stack([fk, fv], axis=2), logf, jnp.stack([sk, sv], axis=2), pool_new, conv_new, lru_new)
    return y, new_state

def setup_inputs(seed: int = 0) -> dict:
    key = jax.random.key(seed)
    ks = jax.random.split(key, 32)
    f32 = jnp.float32
    n_pages = PAST_LEN // PAGE_SIZE
    n_used = DEC_BATCH * n_pages
    n_pool = n_used + n_used // 4

    def nrm(k, shape, s):
        return jax.random.normal(k, shape, f32) * s

    x_prompt = nrm(ks[0], (BATCH, SEQ, D_MODEL), 1.0)
    x_sample = nrm(ks[1], (DEC_BATCH, DEC_SEQ, D_MODEL), 1.0)
    cache_fox_kv = nrm(ks[2], (DEPTH, n_pool, PAGE_SIZE, 2, N_HEADS_FOX, HEAD_DIM), 1.0)
    cache_fox_logf = jax.nn.log_sigmoid(FORGET_BIAS + nrm(ks[3], (DEPTH, n_pool, PAGE_SIZE, N_HEADS_FOX), 1.0))
    cache_sb_kv = nrm(ks[4], (DEPTH, n_pool, PAGE_SIZE, 2, N_HEADS_SB, HEAD_DIM), 1.0)
    state_pool = nrm(ks[5], (DEPTH, DEC_BATCH, POOL_MAX - 1, D_GROUP), 1.0)
    state_conv = nrm(ks[6], (DEPTH, DEC_BATCH, CONV_W - 1, D_GROUP), 1.0)
    state_lru = nrm(ks[7], (DEPTH, DEC_BATCH, D_GROUP), 0.5)
    page_table = jax.random.permutation(ks[8], n_pool)[:n_used].reshape(DEC_BATCH, n_pages).astype(jnp.int32)

    norm1_g = 1.0 + nrm(ks[9], (DEPTH, D_MODEL), 0.02)
    w_in = nrm(ks[10], (DEPTH, D_MODEL, D_IN), D_MODEL ** -0.5)
    pool_w = nrm(ks[11], (DEPTH, len(POOL_WINDOWS), POOL_CH, POOL_CH), POOL_CH ** -0.5)
    pool_scale = 1.0 + nrm(ks[12], (DEPTH, D_GROUP), 0.1)
    conv_w = nrm(ks[13], (DEPTH, CONV_W, D_GROUP), CONV_W ** -0.5)
    conv_b = nrm(ks[14], (DEPTH, D_GROUP), 0.01)
    lru_wa = nrm(ks[15], (DEPTH, LRU_BLOCKS, LRU_BLOCK_DIM, LRU_BLOCK_DIM), LRU_BLOCK_DIM ** -0.5)
    lru_ba = nrm(ks[16], (DEPTH, D_GROUP), 0.01)
    lru_wx = nrm(ks[17], (DEPTH, LRU_BLOCKS, LRU_BLOCK_DIM, LRU_BLOCK_DIM), LRU_BLOCK_DIM ** -0.5)
    lru_bx = nrm(ks[18], (DEPTH, D_GROUP), 0.01)
    a_c = jax.random.uniform(ks[19], (DEPTH, D_GROUP), f32, 0.9, 0.999)
    s_l = a_c ** (1.0 / LRU_C)
    lru_lambda = jnp.log(s_l) - jnp.log1p(-s_l)
    fox_bf = FORGET_BIAS + nrm(ks[20], (DEPTH, N_HEADS_FOX), 0.1)
    fox_q_g = 1.0 + nrm(ks[21], (DEPTH, HEAD_DIM), 0.02)
    fox_k_g = 1.0 + nrm(ks[22], (DEPTH, HEAD_DIM), 0.02)
    out_g = 1.0 + nrm(ks[23], (DEPTH, D_MIX), 0.02)
    w_out = nrm(ks[24], (DEPTH, D_MIX, D_MODEL), D_MIX ** -0.5)
    norm2_g = 1.0 + nrm(ks[25], (DEPTH, D_MODEL), 0.02)
    w_up = nrm(ks[26], (DEPTH, D_MODEL, D_FF), D_MODEL ** -0.5)
    w_down = nrm(ks[27], (DEPTH, D_FF, D_MODEL), D_FF ** -0.5)
    return {'x_prompt': x_prompt, 'x_sample': x_sample, 'cache_fox_kv': cache_fox_kv,
            'cache_fox_logf': cache_fox_logf, 'cache_sb_kv': cache_sb_kv, 'state_pool': state_pool,
            'state_conv': state_conv, 'state_lru': state_lru, 'page_table': page_table,
            'norm1_g': norm1_g, 'w_in': w_in, 'pool_w': pool_w, 'pool_scale': pool_scale,
            'conv_w': conv_w, 'conv_b': conv_b, 'lru_wa': lru_wa, 'lru_ba': lru_ba, 'lru_wx': lru_wx,
            'lru_bx': lru_bx, 'lru_lambda': lru_lambda, 'fox_bf': fox_bf, 'fox_q_g': fox_q_g,
            'fox_k_g': fox_k_g, 'out_g': out_g, 'w_out': w_out, 'norm2_g': norm2_g,
            'w_up': w_up, 'w_down': w_down}

def reference(x_prompt, x_sample, cache_fox_kv, cache_fox_logf, cache_sb_kv, state_pool, state_conv,
              state_lru, page_table, norm1_g, w_in, pool_w, pool_scale, conv_w, conv_b, lru_wa, lru_ba,
              lru_wx, lru_bx, lru_lambda, fox_bf, fox_q_g, fox_k_g, out_g, w_out, norm2_g, w_up, w_down):

    def layer(x, l, pool_prev, conv_prev, lru_h0, past):
        y, st = token_mixers(rms_norm(x, norm1_g[l]), pool_prev, conv_prev, lru_h0, past,
                             w_in[l], pool_w[l], pool_scale[l], conv_w[l], conv_b[l],
                             lru_wa[l], lru_ba[l], lru_wx[l], lru_bx[l], lru_lambda[l],
                             fox_bf[l], fox_q_g[l], fox_k_g[l], out_g[l], w_out[l])
        x = x + y
        hid = jax.nn.relu(jnp.einsum('btd,df->btf', rms_norm(x, norm2_g[l]), w_up[l]))
        x = x + jnp.einsum('btf,fd->btd', hid * hid, w_down[l])
        return x, st

    xp = x_prompt
    bp = xp.shape[0]
    st_p = []
    for l in range(DEPTH):
        xp, st = layer(xp, l,
                       jnp.zeros((bp, POOL_MAX - 1, D_GROUP), xp.dtype),
                       jnp.zeros((bp, CONV_W - 1, D_GROUP), xp.dtype),
                       jnp.zeros((bp, D_GROUP), xp.dtype),
                       None)
        st_p.append(st)

    xs = x_sample
    st_s = []
    for l in range(DEPTH):
        past = (gather_pages(cache_fox_kv[l], page_table),
                gather_pages(cache_fox_logf[l], page_table),
                gather_pages(cache_sb_kv[l], page_table))
        xs, st = layer(xs, l, state_pool[l], state_conv[l], state_lru[l], past)
        st_s.append(st)

    def stk(sts, j):
        return jnp.stack([s[j] for s in sts], axis=0)

    return (xp, xs,
            stk(st_p, 0), stk(st_p, 1), stk(st_p, 2), stk(st_p, 3), stk(st_p, 4), stk(st_p, 5),
            stk(st_s, 0), stk(st_s, 1), stk(st_s, 2), stk(st_s, 3), stk(st_s, 4), stk(st_s, 5))


_drawn_inputs = setup_inputs


def setup_inputs(seed=0):
    import zlib

    import numpy as np

    out = dict(_drawn_inputs(seed))
    spreads = {}
    factors = {'norm1_g': 2.741,
     'lru_ba': 31.395,
     'lru_bx': 31.944,
     'fox_q_g': 8.0,
     'fox_k_g': 4.941,
     'out_g': 3.813,
     'norm2_g': 3.614,
     'conv_b': 3.151}
    for name, (base, spread) in spreads.items():
        noise = np.random.default_rng([zlib.crc32(name.encode()), seed]).standard_normal(out[name].shape)
        drawn = base * np.exp(spread * noise) if base else spread * noise
        out[name] = jnp.asarray(drawn.astype(out[name].dtype))
    for name, factor in factors.items():
        out[name] = (out[name] * factor).astype(out[name].dtype)
    return out
```

```python
from contextlib import ExitStack

import numpy as np
import concourse.bass as bass
from concourse import mybir

F32 = mybir.dt.float32
F32R = mybir.dt.float32r
I32 = mybir.dt.int32
ALU = mybir.AluOpType
ACT = mybir.ActivationFunctionType
AX_X = mybir.AxisListType.X

P = 128
D_MODEL, D_GROUP, D_FF = 2048, 512, 8192
SEQ, DEC_BATCH, DEC_SEQ = 512, 8, 4
NEW = DEC_BATCH * DEC_SEQ
TOK = SEQ + NEW
HALF = TOK // 2
PAGE, PAST = 128, 2048
PAGES = PAST // PAGE
POOL_PAGES = 160
HEADS, HEAD_DIM = 8, 64
PAIRS = HEADS // 2
KEYS = PAST + NEW
KT = D_MODEL // P
GT = D_GROUP // P
ROWS = 32
POOL_MAX, CONV_W = 16, 4
LRU_C = 8.0
EPS = 1e-6
MASKED = -1.0e30

CHUNK = 2048
IN_GROUPS, OUT_GROUPS, FF_CHUNKS = 9, 4, 16
C_IN = 1
C_OUT = C_IN + 4 * IN_GROUPS
C_MLP = C_OUT + 4 * OUT_GROUPS
CHUNKS = C_MLP + 8 * FF_CHUNKS

U_POOL, X_LRU, G_LRU, FQ, FK, FV, SQ, SK, SV = range(9)
Y_POOL, Y_LRU, Y_SB, Y_FOX = U_POOL, X_LRU, G_LRU, FQ

_W = [("norm1", 16), ("norm2", 16), ("out_g", 16), ("pool_scale", 4), ("conv_w", 16), ("conv_b", 4),
      ("ba", 4), ("bx", 4), ("lam", 4), ("fox_q", 1), ("fox_k", 1), ("fox_b", 1), ("head_row", 1)]
PARAM, _at = {}, 0
for _name, _n in _W:
    PARAM[_name] = _at
    _at += _n
N_PARAM = _at

_K = [("ident", P), ("ones", P), ("same_head", P), ("fox_mask", P), ("sb_mask", P),
      ("fox_new", DEC_BATCH * NEW), ("sb_new", DEC_BATCH * NEW), ("pool_rec", GT * POOL_MAX)]
CONST, _at = {}, 0
for _name, _n in _K:
    CONST[_name] = _at
    _at += _n
N_CONST = _at


def build_step(nc, xT, weights, params, consts, neg_head, neg_seq, pool_w, lru_w, state_pool,
               state_conv, state_lru, fox_k, fox_v, sb_k, sb_v, logf_cache, page_rows, page_ids,
               y_out, kv_out, logf_out, pool_p, conv_p, lru_p, pool_s, conv_s, lru_s):
    ctx = ExitStack()

    BASE = 16512
    A_CONST = BASE
    A_RAW = A_CONST + 8192
    A_PROJ = A_RAW + 6 * CHUNK * 4
    SLOT = GT * TOK * 4
    A_ACT = A_PROJ + IN_GROUPS * SLOT
    A_END = 229344
    A_KEEP = A_END - 29824

    def at(name, shape, dt, offset):
        return nc.alloc_sbuf_tensor_at(name, shape, dt, offset=offset)

    class Region:
        def __init__(self, start, end):
            self.next, self.end = start, end

        def take(self, name, shape, dt=F32):
            size = int(np.prod(shape[1:])) * 4
            t = at(name, shape, dt, self.next)
            self.next += (size + 31) // 32 * 32
            assert self.next <= self.end, (name, self.next, self.end)
            return t

    r = Region(A_CONST, A_RAW)
    const = r.take("const", [P, N_CONST])
    par = r.take("par", [P, N_PARAM])
    logit = r.take("logit", [HEADS, TOK])
    derived = r.take("derived", [P, 24])
    idx = r.take("idx", [DEC_BATCH * HEADS, PAGES], I32)
    ids = r.take("ids", [1, DEC_BATCH * PAGES], I32)
    r = Region(A_RAW, A_PROJ)
    w_raw = [r.take(f"w_raw{i}", [P, CHUNK]) for i in range(2)]
    w_hi = [r.take(f"w_hi{i}", [P, CHUNK], F32R) for i in range(2)]
    w_lo = [r.take(f"w_lo{i}", [P, CHUNK], F32R) for i in range(2)]
    proj = at("proj", [P, IN_GROUPS, GT, TOK], F32, A_PROJ)
    act_hi = at("act_hi", [P, KT, TOK], F32R, A_ACT)
    act_lo = at("act_lo", [P, KT, TOK], F32R, A_ACT + KT * TOK * 4)

    x_in = at("x_in", [P, KT, TOK], F32, A_PROJ + 5 * SLOT)
    r = Region(A_PROJ, A_PROJ + SLOT)
    n1_tmp = [r.take(f"n1_tmp{i}", [P, TOK]) for i in range(4)]

    r = Region(A_KEEP, A_END)
    q_pad = [r.take(f"q_pad{x}", [P, DEC_BATCH, PAIRS, ROWS]) for x in range(2)]
    v_new = [r.take(f"v_new{x}", [NEW, D_GROUP]) for x in range(2)]
    k_new = [r.take(f"k_new{x}", [P, PAIRS, NEW]) for x in range(2)]
    log_decay = r.take("log_decay", [DEC_BATCH * HEADS, KEYS])
    neg_seq_sb = r.take("neg_seq_sb", [DEC_BATCH * HEADS, DEC_BATCH * P])
    neg_head_sb = r.take("neg_head_sb", [HEADS, HEADS * P])

    r = Region(A_ACT, A_KEEP)
    lx = r.take("lx", [P, GT, TOK])
    lr = r.take("lr", [P, GT, TOK])
    li = r.take("li", [P, GT, TOK])
    la = r.take("la", [P, GT, TOK])
    lm = r.take("lm", [P, GT, TOK])
    ext_conv = r.take("ext_conv", [P, GT, DEC_BATCH, CONV_W - 1 + DEC_SEQ])
    seq_a = r.take("seq_a", [P, GT, DEC_BATCH, DEC_SEQ + 1])
    seq_u = r.take("seq_u", [P, GT, DEC_BATCH, DEC_SEQ + 1])
    h0 = r.take("h0", [P, GT, DEC_BATCH])
    last_h = r.take("last_h", [P, GT])
    seq_last = r.take("seq_last", [P, GT, DEC_BATCH])
    seq_h = r.take("seq_h", [P, GT, DEC_BATCH, DEC_SEQ + 1])
    r = Region(A_KEEP, A_END)
    pool_w_sb = r.take("pool_w_sb", [P, GT, P])
    lru_w_sb = r.take("lru_w_sb", [P, 2, GT, P])
    ext_pool = r.take("ext_pool", [P, GT, DEC_BATCH, POOL_MAX - 1 + DEC_SEQ])
    psum_a = r.take("psum_a", [P, POOL_MAX + SEQ])
    psum_b = r.take("psum_b", [P, POOL_MAX + SEQ])
    pseq_a = r.take("pseq_a", [P, DEC_BATCH, POOL_MAX - 1 + DEC_SEQ])
    pseq_b = r.take("pseq_b", [P, DEC_BATCH, POOL_MAX - 1 + DEC_SEQ])
    pool_d = [r.take(f"pool_d{i}", [P, TOK]) for i in range(2)]

    r = Region(A_ACT, A_KEEP)
    v_tok = [r.take(f"v_tok{x}", [P, GT, D_GROUP]) for x in range(2)]
    pf = [r.take(f"pf{i}", [P, SEQ]) for i in range(3)]
    ps = [r.take(f"ps{i}", [P, SEQ]) for i in range(2)]
    pa = [r.take(f"pa{i}", [P, SEQ]) for i in range(2)]
    pc = [r.take(f"pc{i}", [P, SEQ]) for i in range(2)]
    ptf = [r.take(f"ptf{i}", [P, SEQ]) for i in range(2)]
    pts = [r.take(f"pts{i}", [P, SEQ]) for i in range(2)]
    stat = r.take("stat", [P, 3, 4])
    c_prompt = r.take("c_prompt", [HEADS, SEQ])
    r = Region(A_PROJ + G_LRU * SLOT, A_PROJ + (G_LRU + 1) * SLOT)
    sq_tmp = [r.take(f"sq_tmp{i}", [P, TOK]) for i in range(2)]
    rs_tmp = [r.take(f"rs_tmp{i}", [P, TOK]) for i in range(2)]

    r = Region(A_PROJ + 4 * SLOT, A_KEEP)
    v_ring = [r.take(f"v_ring{x}", [P, PAGES, D_GROUP]) for x in range(2)]
    s_fox = r.take("s_fox", [P, KEYS])
    s_z = r.take("s_z", [P, KEYS])
    s_l = r.take("s_l", [P, KEYS])
    r = Region(A_RAW, A_PROJ)
    k_ring = r.take("k_ring", [P, 4, 4, PAIRS, PAGE])
    s_r = r.take("s_r", [P, KEYS])
    p_t = r.take("p_t", [P, 2, 4, P])
    o_sb = r.take("o_sb", [P, P])
    q_now = [r.take(f"q_now{x}", [P, PAIRS, ROWS]) for x in range(2)]
    neg_now = r.take("neg_now", [DEC_BATCH * HEADS, P])
    dstat = r.take("dstat", [P, 4])

    hid_hi = at("hid_hi", [P, 2, GT, TOK], F32R, A_PROJ)
    hid_lo = at("hid_lo", [P, 2, GT, TOK], F32R, A_PROJ + 2 * SLOT)
    x_res = at("x_res", [P, KT, TOK], F32, A_PROJ + 4 * SLOT)
    r = Region(A_PROJ + 8 * SLOT, A_ACT)
    n2_tmp = [r.take(f"n2_tmp{i}", [P, TOK]) for i in range(4)]

    bank = ctx.enter_context(nc.psum_tensor("bank", [P, 8, 512], F32))

    def pair_of(n):
        q = n % 4
        return bank[:, 2 * q:2 * q + 2, 0:HALF]

    def cc(name, a=0, n=1):
        return const[:, CONST[name] + a:CONST[name] + a + n]

    ident, ones, same_head = cc("ident", 0, P), cc("ones", 0, P), cc("same_head", 0, P)

    def pcol(name, k=0):
        return par[:, PARAM[name] + k:PARAM[name] + k + 1]

    D_NBA, D_NBX, D_SPL, D_FQ = 0, 4, 8, 12
    D_LE = 16

    def sem(name):
        return ctx.enter_context(nc.semaphore(name))

    consts_in = sem("consts_in")
    x_loaded = [sem(f"x_loaded{i}") for i in range(4)]
    w_loaded = [sem(f"w_loaded{i}") for i in range(2)]
    w_high = sem("w_high")
    w_low = sem("w_low")
    strips = sem("strips")
    evac_a = sem("evac_a")
    evac_b = sem("evac_b")
    squares = sem("squares")
    summed = sem("summed")
    sums_out = sem("sums_out")
    rstd = sem("rstd")
    normed = sem("normed")
    a_high = sem("a_high")
    a_low = sem("a_low")
    act_own = sem("act_own")
    dve_own = sem("dve_own")
    pool_own = sem("pool_own")
    stage_end = sem("stage_end")
    small_in = sem("small_in")
    ext_ready = sem("ext_ready")
    src_out = sem("src_out")
    early_outs = sem("early_outs")
    lam_ln = sem("lam_ln")
    vecs_ready = sem("vecs_ready")
    conv_ready = sem("conv_ready")
    gate_mm = sem("gate_mm")
    gate_read = sem("gate_read")
    gates_sig = sem("gates_sig")
    decay_act = sem("decay_act")
    mult_sq = sem("mult_sq")
    mult_ready = sem("mult_ready")
    gelu_in = sem("gelu_in")
    gelu_arg = sem("gelu_arg")
    gelu_tanh = sem("gelu_tanh")
    lru_states = sem("lru_states")
    pool_diff = sem("pool_diff")
    table_in = sem("table_in")
    signs_in = sem("signs_in")
    lf_rows = sem("lf_rows")
    lf_gather = sem("lf_gather")
    lf_ln = sem("lf_ln")
    new_lf = sem("new_lf")
    c_ready = sem("c_ready")
    head_sq = sem("head_sq")
    head_sum = sem("head_sum")
    head_rs = sem("head_rs")
    head_norm = sem("head_norm")
    q_scaled = sem("q_scaled")
    v_turned = sem("v_turned")
    v_stored = sem("v_stored")
    q_cleared = sem("q_cleared")
    outs = sem("outs")
    f_score, s_score = sem("f_score"), sem("s_score")
    f_max = sem("f_max")
    f_exp = sem("f_exp")
    f_prob, s_prob = sem("f_prob"), sem("s_prob")
    s_ln = sem("s_ln")
    s_diff = sem("s_diff")
    f_pt, s_pt = sem("f_pt"), sem("s_pt")
    f_ptsb, s_ptsb = sem("f_ptsb"), sem("s_ptsb")
    f_av, s_av = sem("f_av"), sem("s_av")
    f_y, s_y = sem("f_y"), sem("s_y")
    q_staged, s_staged = sem("q_staged"), sem("s_staged")
    k_loaded = [sem(f"k_loaded{i}") for i in range(4)]
    v_loaded = [[sem(f"v_loaded{x}_{i}") for i in range(4)] for x in range(2)]
    ld_ready = sem("ld_ready")
    d_rinv = sem("d_rinv")
    d_sp = sem("d_sp")
    d_sum = sem("d_sum")
    d_score = sem("d_score")
    d_copied = sem("d_copied")
    d_max = sem("d_max")
    d_exp = sem("d_exp")
    d_ln = sem("d_ln")
    d_diff = sem("d_diff")
    d_wgt = sem("d_wgt")
    d_pt = sem("d_pt")
    d_ptsb = sem("d_ptsb")
    d_av = sem("d_av")
    d_o = sem("d_o")
    d_ot = sem("d_ot")
    d_y = sem("d_y")
    again_in = sem("again_in")
    again_high = sem("again_high")
    again_low = sem("again_low")
    xr_in = sem("xr_in")
    sq_in = sem("sq_in")
    hid_h = sem("hid_h")
    hid_l = sem("hid_l")
    n_outs = [0]

    class Own:
        def __init__(self, eng, s):
            self.eng, self.s, self.n = eng, s, 0

        def then(self, ins):
            ins.then_inc(self.s, 1)
            self.n += 1
            return self.n

        def wait(self, n=None):
            self.eng.wait_ge(self.s, self.n if n is None else n)

    ENGINES = 5

    def end_stage(eng, n):
        eng.sem_inc(stage_end, 1)
        eng.wait_ge(stage_end, ENGINES * n)


    def load_chunk(sp, c0, i=0, step=0):
        if not (c0 < 2 and step == 0):
            sp.wait_ge(w_low, c0 - 1 + step * i)
        sp.dma_start(w_raw[c0 % 2][:], weights[bass.ds(c0 + step * i, 1)].rearrange("a p n -> (a p) n")
                     ).then_inc(w_loaded[c0 % 2], 16)

    def high_part(act, c0, i=0, step=0):
        act.wait_ge(w_loaded[c0 % 2], 16 * (c0 // 2 + 1) + 8 * step * i)
        if not (c0 < 2 and step == 0):
            act.wait_ge(strips, 4 * (c0 - 1) + 4 * step * i)
        nc.scalar.activation(w_hi[c0 % 2][:], w_raw[c0 % 2][:], ACT.Copy).then_inc(w_high, 1)

    def low_part(dve, c0, i=0, step=0):
        dve.wait_ge(w_high, c0 + 1 + step * i)
        nc.vector.tensor_tensor(w_lo[c0 % 2][:], w_raw[c0 % 2][:], w_hi[c0 % 2][:].bitcast(F32),
                                ALU.subtract).then_inc(w_low, 1)

    def multiply(pe, c0, rhs_hi, rhs_lo, first, last, i=0, step=0, tile0=None, split=None):
        if split:
            pe.wait_ge(a_low, split)
        pe.wait_ge(w_low, c0 + 1 + step * i)
        hi = w_hi[c0 % 2][:].rearrange("p (k n) -> p k n", k=4)
        lo = w_lo[c0 % 2][:].rearrange("p (k n) -> p k n", k=4)
        for m in range(4):
            n, per = tile0
            n += m
            out = pair_of(n)
            if first:
                pe.wait_ge(evac_a, n + 1 + per * i)
                pe.wait_ge(evac_b, n + 1 + per * i)
            for k in range(4):
                cols = slice(m * P, m * P + P)
                begin, end = first and k == 0, last and k == 3
                for h in range(2):
                    t = slice(h * HALF, h * HALF + HALF)
                    nc.tensor.matmul(out[:, h], hi[:, k, cols], rhs_hi[:, k, t], start=begin, stop=False)
                for h in range(2):
                    t = slice(h * HALF, h * HALF + HALF)
                    nc.tensor.matmul(out[:, h], hi[:, k, cols], rhs_lo[:, k, t], start=False, stop=False)
                for h in range(2):
                    t = slice(h * HALF, h * HALF + HALF)
                    ins = nc.tensor.matmul(out[:, h], lo[:, k, cols], rhs_hi[:, k, t], start=False, stop=end)
            ins.then_inc(strips, 1)

    def square_tiles(act, src, t0, tiles, tmp, k0, ready):
        for t in tiles:
            k = k0 + t
            ready(act, t)
            if t >= t0 + 2:
                act.wait_ge(summed, k - 1)
            elif t0 > 0:
                act.wait_ge(a_low, k - 1)
            nc.scalar.activation(tmp[t % 2][:], src(t), ACT.Square).then_inc(squares, 1)

    def norm_act(act, own, src, jobs, tmp, k0, j0, ready, between=None, squared=False):
        for j, (t0, n) in enumerate(jobs):
            if not squared:
                square_tiles(act, src, t0, range(t0, t0 + n), tmp, k0, ready)
            if between:
                between()
            act.wait_ge(sums_out, j0 + j + 1)
            if t0 > 0:
                act.wait_ge(normed, k0 + t0)
            rs = tmp[3][:].rearrange("p (h t) -> p h t", h=2)
            nc.scalar.activation(rs, bank[:, 0:2, 0:HALF], ACT.Ln, scale=1.0 / (n * P), bias=EPS
                                 ).then_inc(own.s, 1)
            own.n += 1
            own.wait()
            nc.scalar.activation(rs, rs, ACT.Exp, scale=-0.5).then_inc(rstd, 1)
            for t in range(t0, t0 + n):
                act.wait_ge(normed, k0 + t + 1)
                nc.scalar.activation(act_hi[:, t], tmp[t % 2][:], ACT.Copy).then_inc(a_high, 1)

    def sum_tiles(dve, t0, tiles, tmp, k0):
        for t in tiles:
            dve.wait_ge(squares, k0 + t + 1)
            if t == t0:
                nc.vector.tensor_copy(tmp[2][:], tmp[t % 2][:]).then_inc(summed, 1)
            else:
                dve.wait_ge(summed, k0 + t)
                nc.vector.tensor_tensor(tmp[2][:], tmp[2][:], tmp[t % 2][:], ALU.add).then_inc(summed, 1)

    def norm_dve(dve, src, gain, jobs, tmp, k0, j0, between=None, summed_up=False):
        for j, (t0, n) in enumerate(jobs):
            if not summed_up:
                if j > 0:
                    dve.wait_ge(sums_out, j0 + j)
                sum_tiles(dve, t0, range(t0, t0 + n), tmp, k0)
            if between:
                between()
            dve.wait_ge(rstd, j0 + j + 1)
            dve.wait_ge(summed, k0 + t0 + n)

            def low(t):
                dve.wait_ge(a_high, k0 + t + 1)
                nc.vector.tensor_tensor(act_lo[:, t], tmp[t % 2][:], act_hi[:, t].bitcast(F32),
                                        ALU.subtract).then_inc(a_low, 1)

            for t in range(t0, t0 + n):
                if t >= t0 + 2:
                    dve.wait_ge(a_low, k0 + t - 1)
                nc.vector.scalar_tensor_tensor(out=tmp[t % 2][:], in0=src(t), scalar=gain(t), in1=tmp[3][:],
                                               op0=ALU.mult, op1=ALU.mult).then_inc(normed, 1)
                if t > t0:
                    low(t - 1)
            low(t0 + n - 1)
            dve.wait_ge(a_low, k0 + t0 + n)

    def norm_pe(pe, jobs, tmp, k0, j0):
        for j, (t0, n) in enumerate(jobs):
            pe.wait_ge(summed, k0 + t0 + n)
            if j0 + j > 0:
                pe.wait_ge(rstd, j0 + j)
            for h in range(2):
                ins = nc.tensor.matmul(bank[:, h, 0:HALF], ones, tmp[2][:, h * HALF:h * HALF + HALF],
                                       start=True, stop=True)
            ins.then_inc(sums_out, 1)

    NORM1 = [(0, KT)]
    NORMY = [(GT * g, GT) for g in range(4)]
    NORM2 = [(0, KT)]
    y_slot = [Y_POOL, Y_LRU, Y_FOX, Y_SB]

    def y_src(t):
        return proj[:, y_slot[t // GT], t % GT]

    T_OUT = 1 + 4 * IN_GROUPS
    T_MLP = T_OUT + 4 * OUT_GROUPS
    T_LAST = T_MLP + 20 * FF_CHUNKS - 16
    UNITS = 4 * HEADS

    block = ctx.enter_context(nc.Block())

    @block.sync
    def _(sp):
        sp.dma_start(par[:], params).then_inc(consts_in, 16)
        sp.dma_start(const[:], consts).then_inc(consts_in, 16)
        for q in range(4):
            sp.dma_start(x_in[:, 4 * q:4 * q + 4], xT[:, 4 * q:4 * q + 4]).then_inc(x_loaded[q], 16)
        load_chunk(sp, 0)
        load_chunk(sp, 1)
        with sp.Fori(0, (C_OUT - 1) // 2) as i:
            load_chunk(sp, 2, i, 2)
            load_chunk(sp, 3, i, 2)
        load_chunk(sp, C_OUT + 1)
        end_stage(sp, 1)

        sp.dma_start(pool_w_sb[:], pool_w).then_inc(small_in, 16)
        sp.dma_start(lru_w_sb[:], lru_w).then_inc(small_in, 16)
        sp.dma_start(ext_pool[:, :, :, 0:POOL_MAX - 1], state_pool).then_inc(small_in, 16)
        sp.dma_start(ext_conv[:, :, :, 0:CONV_W - 1], state_conv).then_inc(small_in, 16)
        sp.dma_start(h0[:], state_lru).then_inc(small_in, 16)
        sp.dma_start(pool_p, proj[:, U_POOL, :, SEQ - POOL_MAX + 1:SEQ]).then_inc(src_out, 16)
        sp.dma_start(conv_p, proj[:, X_LRU, :, SEQ - CONV_W + 1:SEQ]).then_inc(src_out, 16)
        sp.dma_start(kv_out[3], proj[:, SV]).then_inc(outs, 16)
        sp.dma_start(kv_out[2], proj[:, SK]).then_inc(outs, 16)
        sp.dma_start(kv_out[1], proj[:, FV]).then_inc(outs, 16)
        n_outs[0] += 3
        sp.wait_ge(ext_ready, 2)
        sp.dma_start(pool_s, ext_pool[:, :, :, DEC_SEQ:]).then_inc(early_outs, 16)
        sp.dma_start(conv_s, ext_conv[:, :, :, DEC_SEQ:]).then_inc(early_outs, 16)
        sp.wait_ge(lru_states, 2)
        sp.dma_start(lru_p, last_h[:]).then_inc(early_outs, 16)
        sp.dma_start(lru_s, seq_last[:]).then_inc(early_outs, 16)
        sp.wait_ge(early_outs, 4 * 16)
        sp.wait_ge(src_out, 2 * 16)
        end_stage(sp, 2)

        sp.dma_start(neg_head_sb[:], neg_head).then_inc(signs_in, 16)
        sp.dma_start(neg_seq_sb[:], neg_seq).then_inc(signs_in, 16)
        sp.wait_ge(head_norm, 8)
        sp.dma_start(kv_out[0], proj[:, FK]).then_inc(outs, 16)
        sp.wait_ge(new_lf, 1)
        sp.dma_start(logf_out, logit[:]).then_inc(outs, 16)
        n_outs[0] += 2
        sp.wait_ge(lf_rows, 1)
        for b in range(DEC_BATCH):
            sp.dma_start(log_decay[HEADS * b:HEADS * b + HEADS, PAST + DEC_SEQ * b:PAST + DEC_SEQ * b + DEC_SEQ],
                         logit[:, SEQ + DEC_SEQ * b:SEQ + DEC_SEQ * b + DEC_SEQ]).then_inc(table_in, 16)
        sp.wait_ge(outs, 16 * n_outs[0])
        sp.wait_ge(table_in, 16 * 8)

        sp.dma_start(ids[:], page_ids).then_inc(table_in, 16)
        sp.wait_ge(table_in, 16 * 9)

        def load_keys(b, x, cache, first):
            for blk in range(4):
                for j in range(4):
                    page = sp.value_load(ids[0:1, bass.ds(PAGES * b + 4 * blk + j, 1)], min_val=0, max_val=POOL_PAGES - 1)
                    if j == 0 and not first:
                        sp.wait_ge(d_score, 10 * b + 5 * x + blk - 4)
                    sp.dma_start(k_ring[:, blk, j].rearrange("p h k -> p (h k)"),
                                 cache[bass.ds(page, 1)].rearrange("a p n -> (a p) n")).then_inc(k_loaded[blk], 16)

        load_keys(0, 0, fox_k, True)
        end_stage(sp, 3)
        load_keys(0, 1, sb_k, False)
        with sp.Fori(1, DEC_BATCH) as b:
            load_keys(b, 0, fox_k, False)
            load_keys(b, 1, sb_k, False)
        end_stage(sp, 4)

        for c in (C_OUT, C_OUT + 1):
            sp.dma_start(w_raw[c % 2][:], weights[c:c + 1].rearrange("a p n -> (a p) n")).then_inc(again_in, 16)
        for q in range(4):
            sp.dma_start(x_res[:, 4 * q:4 * q + 4], xT[:, 4 * q:4 * q + 4]).then_inc(xr_in, 16)
        sp.wait_ge(again_low, 2)
        with sp.Fori(0, (CHUNKS - C_OUT - 2) // 2) as i:
            load_chunk(sp, C_OUT + 2, i, 2)
            load_chunk(sp, C_OUT + 3, i, 2)
        if (CHUNKS - C_OUT) % 2:
            load_chunk(sp, CHUNKS - 1)
        for q in range(4):
            sp.wait_ge(evac_b, 4 + T_LAST + 4 * (q + 1))
            sp.dma_start(y_out[:, 4 * q:4 * q + 4], x_res[:, 4 * q:4 * q + 4]).then_inc(outs, 16)
            n_outs[0] += 1
        sp.wait_ge(outs, 16 * n_outs[0])


    @block.gpsimd
    def _(pool):
        own = Own(pool, pool_own)
        pool.wait_ge(consts_in, 32)
        end_stage(pool, 1)

        PRE = POOL_MAX - 1
        own.then(nc.gpsimd.memset(psum_a[:, 0:POOL_MAX], 0.0))
        own.then(nc.gpsimd.memset(psum_b[:, 0:POOL_MAX], 0.0))
        pool.wait_ge(small_in, 16 * 5)
        nc.gpsimd.tensor_copy(ext_pool[:, :, :, PRE:],
                              proj[:, U_POOL, :, SEQ:].rearrange("p g (b t) -> p g b t", b=DEC_BATCH)
                              ).then_inc(ext_ready, 1)
        for g in range(GT):
            w = 2 ** (g + 1)
            u = proj[:, U_POOL, g]
            if g >= 2:
                pool.wait_ge(gate_mm, 8 + g - 1)
            d = pool_d[g % 2]
            own.wait()
            own.then(nc.gpsimd.tensor_copy(psum_a[:, POOL_MAX:], u[:, 0:SEQ]))
            own.wait()
            pool.wait_ge(ext_ready, 2)
            own.then(nc.gpsimd.tensor_copy(pseq_a[:], ext_pool[:, g]))
            a, b, sa, sb_ = psum_a, psum_b, pseq_a, pseq_b
            for level in range(g + 1):
                back = 2 ** level
                own.wait()
                own.then(nc.gpsimd.tensor_tensor(b[:, POOL_MAX:], a[:, POOL_MAX:],
                                                 a[:, POOL_MAX - back:POOL_MAX + SEQ - back], ALU.add))
                lo = 2 * back - 1
                own.then(nc.gpsimd.tensor_tensor(sb_[:, :, lo:], sa[:, :, lo:], sa[:, :, lo - back:PRE + DEC_SEQ - back],
                                                 ALU.add))
                a, b, sa, sb_ = b, a, sb_, sa
            own.wait()
            own.then(nc.gpsimd.tensor_scalar(d[:, 0:SEQ], a[:, POOL_MAX:], 1.0 / w, None, ALU.mult))
            own.then(nc.gpsimd.tensor_scalar(d[:, SEQ:].rearrange("p (b t) -> p b t", b=DEC_BATCH), sa[:, :, PRE:],
                                             1.0 / w, None, ALU.mult))
            own.wait()
            own.then(nc.gpsimd.tensor_tensor(d[:, 0:POOL_MAX], a[:, POOL_MAX:2 * POOL_MAX],
                                             cc("pool_rec", g * POOL_MAX, POOL_MAX), ALU.mult))
            own.wait()
            nc.gpsimd.tensor_tensor(d[:], d[:], u, ALU.subtract).then_inc(pool_diff, 1)
        pool.wait_ge(pool_diff, GT)
        end_stage(pool, 2)

        own.then(nc.gpsimd.memset(log_decay[:, PAST:], 0.0))
        for x in range(2):
            own.then(nc.gpsimd.memset(q_pad[x][:], 0.0))
        own.wait()
        pool.sem_inc(q_cleared, 1)
        pool.dma_start(idx[:], page_rows).then_inc(lf_gather, 16)
        pool.wait_ge(lf_gather, 16)
        own.then(nc.gpsimd.tensor_scalar(idx[:], idx[:], float(HEADS), par[0:DEC_BATCH * HEADS, PARAM["head_row"]:PARAM["head_row"] + 1],
                                         ALU.mult, ALU.add))
        own.wait()
        for j in range(PAGES):
            nc.gpsimd.indirect_dma_start(log_decay[:, PAGE * j:PAGE * j + PAGE], None, logf_cache,
                                         bass.IndirectOffsetOnAxis(ap=idx[:, j:j + 1], axis=0)).then_inc(lf_gather, 16)
        pool.wait_ge(lf_gather, 16 * (PAGES + 1))
        pool.sem_inc(lf_rows, 1)
        end_stage(pool, 3)

        def load_values(b, x, cache, first):
            for blk in range(4):
                for j in range(4):
                    page = pool.value_load(ids[0:1, bass.ds(PAGES * b + 4 * blk + j, 1)], min_val=0, max_val=POOL_PAGES - 1)
                    if j == 0 and not first:
                        pool.wait_ge(d_av, 10 * b + 5 * x + blk - 9)
                    pool.dma_start(v_ring[x][:, 4 * blk + j], cache[bass.ds(page, 1)].rearrange("a p n -> (a p) n")
                                 ).then_inc(v_loaded[x][blk], 16)

        def stage(b, first):
            if not first:
                pool.wait_ge(d_score, 10 * b - 5)
            nc.gpsimd.tensor_copy(q_now[0][:], q_pad[0][:, bass.ds(b, 1)].rearrange("p a h r -> p (a h) r")
                                  ).then_inc(q_staged, 1)
            nc.gpsimd.tensor_copy(neg_now[:], neg_seq_sb[:, bass.ds(b * P, P)]).then_inc(q_staged, 1)
            if not first:
                pool.wait_ge(d_score, 10 * b)
            nc.gpsimd.tensor_copy(q_now[1][:], q_pad[1][:, bass.ds(b, 1)].rearrange("p a h r -> p (a h) r")
                                  ).then_inc(s_staged, 1)
            load_values(b, 0, fox_v, first)
            load_values(b, 1, sb_v, first)

        pool.wait_ge(table_in, 16 * 9)
        stage(0, True)
        with pool.Fori(1, DEC_BATCH) as b:
            stage(b, False)
        end_stage(pool, 4)

    @block.scalar
    def _(act):
        own = Own(act, act_own)

        def f(out, in_, func, **kw):
            return nc.scalar.activation(out, in_, func, **kw)

        act.sem_inc(evac_a, 4)
        act.wait_ge(consts_in, 32)

        def first_parts():
            high_part(act, 0)
            high_part(act, 1)

        norm_act(act, own, lambda t: x_in[:, t], NORM1, n1_tmp, 0, 0,
                 lambda e, t: e.wait_ge(x_loaded[t // 4], 16), first_parts)
        act.wait_ge(strips, 4)
        f(logit[:, 0:HALF], bank[0:HEADS, 0, 0:HALF], ACT.Copy).then_inc(evac_a, 1)
        high_part(act, 2)

        with act.Fori(0, IN_GROUPS) as g:
            for j in range(4):
                if j == 3:
                    for m in range(4):
                        act.wait_ge(strips, 4 * (C_IN + 3) + m + 1 + 16 * g)
                        f(proj[:, bass.ds(g, 1), m, 0:HALF].rearrange("p a t -> p (a t)"), pair_of(1 + m)[:, 0], ACT.Copy
                          ).then_inc(evac_a, 1)
                high_part(act, C_IN + j + 2, g, 4)
        act.wait_ge(evac_a, 4 + T_OUT)
        act.wait_ge(w_high, C_OUT + 2)
        end_stage(act, 1)

        e1 = derived[:, 16:20]
        lam = par[:, PARAM["lam"]:PARAM["lam"] + 4]
        own.then(f(e1, lam, ACT.Abs))
        own.wait()
        own.then(f(e1, e1, ACT.Exp, scale=-1.0))
        own.wait()
        f(e1, e1, ACT.Ln, bias=1.0).then_inc(lam_ln, 1)
        act.wait_ge(vecs_ready, 1)
        for n in range(8):
            g, dst = n % 4, (lr, li)[n // 4]
            act.wait_ge(gate_mm, n + 1)
            f(dst[:, g].rearrange("p (h t) -> p h t", h=2), pair_of(n), ACT.Exp, scale=-1.0,
              bias=derived[:, n:n + 1]).then_inc(gate_read, 1)
        act.wait_ge(gates_sig, 1)
        for g in range(GT):
            f(la[:, g], lr[:, g], ACT.Exp, scale=derived[:, 8 + g:9 + g]).then_inc(decay_act, 1)
        for g in range(GT):
            f(lm[:, g], lr[:, g], ACT.Tanh, scale=derived[:, 12 + g:13 + g]).then_inc(decay_act, 1)
        act.wait_ge(mult_sq, 1)
        f(lm[:], lm[:], ACT.Sqrt).then_inc(mult_ready, 1)
        act.wait_ge(gelu_arg, 1)
        f(li[:], proj[:, G_LRU], ACT.Square).then_inc(gelu_in, 1)
        act.wait_ge(gelu_arg, 2)
        f(li[:], li[:], ACT.Tanh, scale=0.7978845608028654).then_inc(gelu_tanh, 1)
        act.wait_ge(src_out, 32)
        for g in range(GT):
            act.wait_ge(gate_mm, 8 + g + 1)
            f(proj[:, Y_POOL, g].rearrange("p (h t) -> p h t", h=2), pair_of(g), ACT.Copy,
              scale=pcol("pool_scale", g)).then_inc(gate_read, 1)
        act.wait_ge(gate_read, 12)
        end_stage(act, 2)

        nc.scalar.preload_act_table_set("natural_log_exp_and_others")
        lf_e = rs_tmp[0][0:HEADS]
        own.then(f(lf_e, logit[:], ACT.Abs, bias=par[0:HEADS, PARAM["fox_b"]:PARAM["fox_b"] + 1]))
        own.wait()
        own.then(f(lf_e, lf_e, ACT.Exp, scale=-1.0))
        own.wait()
        f(lf_e, lf_e, ACT.Ln, bias=1.0).then_inc(lf_ln, 1)
        act.wait_ge(new_lf, 1)

        def v_store(n):
            act.wait_ge(v_turned, n + 1)
            x, tt = divmod(n, 5)
            if tt < 4:
                f(v_tok[x][:, tt], bank[:, 4 + n % 4], ACT.Copy).then_inc(v_stored, 1)
            else:
                f(v_new[x][:], bank[0:NEW, 4 + n % 4], ACT.Copy).then_inc(v_stored, 1)

        for t in range(8):
            src = proj[:, (FQ, FK)[t // 4], t % 4]
            if t >= 2:
                act.wait_ge(head_sum, t - 1)
            f(sq_tmp[t % 2][:], src, ACT.Square).then_inc(head_sq, 1)
            v_store(t)
            act.wait_ge(head_sum, t + 1)
            if t >= 2:
                act.wait_ge(head_norm, t - 1)
            rs = rs_tmp[t % 2][:].rearrange("p (h t) -> p h t", h=2)
            own.then(f(rs, bank[:, 2 * (t % 2):2 * (t % 2) + 2, 0:HALF], ACT.Ln, scale=1.0 / HEAD_DIM, bias=EPS))
            own.wait()
            f(rs, rs, ACT.Exp, scale=-0.5).then_inc(head_rs, 1)
        v_store(8)
        v_store(9)

        for i in range(UNITS + 4):
            if i < UNITS:
                n = (i % 4 + 1) * P
                act.wait_ge(f_max, i + 1)
                if i >= 3:
                    act.wait_ge(f_pt, i - 2)
                f(pf[i % 3][:, 0:n], bank[:, i % 2, 0:n], ACT.Exp, bias=stat[:, i % 3, 0:1],
                  accum_out=stat[:, i % 3, 1:2]).then_inc(f_exp, 1)
                act.wait_ge(s_score, i + 1)
                if i >= 2:
                    act.wait_ge(s_prob, i - 1)
                a = pa[i % 2][:, 0:n]
                own.then(f(a, bank[:, 2 + i % 2, 0:n], ACT.Abs))
                own.wait()
                own.then(f(a, a, ACT.Exp, scale=-1.0))
                own.wait()
                f(a, a, ACT.Ln, bias=1.0).then_inc(s_ln, 1)
            if 1 <= i <= UNITS:
                k = i - 1
                n = (k % 4 + 1) * P
                act.wait_ge(s_diff, k + 1)
                if k >= 2:
                    act.wait_ge(s_pt, k - 1)
                f(ps[k % 2][:, 0:n], pa[k % 2][:, 0:n], ACT.Exp).then_inc(s_prob, 1)
            if i >= 4:
                k = i - 4
                h, q = divmod(k, 4)
                o = HEAD_DIM * (h % 2)
                act.wait_ge(s_av, k + 1)
                f(proj[o:o + HEAD_DIM, Y_SB, h // 2, P * q:P * q + P], bank[o:o + HEAD_DIM, 7, 0:P], ACT.Copy
                  ).then_inc(s_y, 1)
        act.wait_ge(s_y, UNITS)
        end_stage(act, 3)

        def fox_exp(b):
            act.wait_ge(d_max, b + 1)
            f(s_fox[:], s_fox[:], ACT.Exp, bias=dstat[:, 0:1], accum_out=dstat[:, 1:2]).then_inc(d_exp, 1)

        def sb_logs(b, base, per, first=False):
            act.wait_ge(d_copied, 10 * b + 10)
            s = act_own
            f(s_l[:], s_z[:], ACT.Abs).then_inc(s, 1)
            turn_store(b, 0, (0, 1), first)
            act.wait_ge(s, base + 1 + per)
            f(s_l[:], s_l[:], ACT.Exp, scale=-1.0).then_inc(s, 1)
            turn_store(b, 0, (2,), first)
            act.wait_ge(s, base + 2 + per)
            f(s_l[:], s_l[:], ACT.Ln, bias=1.0).then_inc(d_ln, 1)
            turn_store(b, 0, (3, 4), first)

        def sb_weights(b):
            act.wait_ge(d_diff, b + 1)
            f(s_z[:], s_z[:], ACT.Exp).then_inc(d_wgt, 1)

        def turn_store(b, x, groups, first=False):
            for g in groups:
                G = 10 * b + 5 * x + g
                act.wait_ge(d_pt, G + 1)
                if g >= 2:
                    act.wait_ge(d_av, G - 1)
                elif not first:
                    act.wait_ge(d_av, G - 2 * g)
                if g < 4:
                    f(p_t[:, g % 2], bank[:, 5 + g % 2].rearrange("p (j r) -> p j r", j=4), ACT.Copy).then_inc(d_ptsb, 1)
                else:
                    f(p_t[0:NEW, 0, 0], bank[0:NEW, 5, 0:P], ACT.Copy).then_inc(d_ptsb, 1)

        base = own.n
        fox_exp(0)
        sb_logs(0, base, 0, True)
        sb_weights(0)
        with act.Fori(1, DEC_BATCH) as b:
            fox_exp(b)
            turn_store(b - 1, 1, range(5))
            sb_logs(b, base, 2 * b)
            sb_weights(b)
        turn_store(DEC_BATCH - 1, 1, range(5))
        own.n = base + 2 * DEC_BATCH
        act.wait_ge(d_ptsb, 10 * DEC_BATCH)
        end_stage(act, 4)

        act.wait_ge(again_in, 2 * 16)
        for c in (C_OUT, C_OUT + 1):
            f(w_hi[c % 2][:], w_raw[c % 2][:], ACT.Copy).then_inc(again_high, 1)
        norm_act(act, own, y_src, NORMY, n2_tmp, KT, 1, lambda e, t: None)
        for g in range(OUT_GROUPS):
            for j in range(4):
                high_part(act, C_OUT + 4 * g + j + 2)
            square_tiles(act, lambda t: x_res[:, t], 0, range(4 * g, 4 * g + 4), n2_tmp, 2 * KT,
                         lambda e, t: e.wait_ge(evac_b, 4 + T_OUT + t + 1))
        norm_act(act, own, lambda t: x_res[:, t], NORM2, n2_tmp, 2 * KT, 5, None, squared=True)

        def up(c0, t0, h0_, slot, i=0, step=0):
            per = 20 * step // 8
            hp = step // 2
            for j in range(4):
                if j == 3:
                    def relu(m):
                        act.wait_ge(strips, 4 * (c0 + 3) + m + 1 + 4 * step * i)
                        if not (h0_ + m < 2 and step == 0):
                            act.wait_ge(sq_in, h0_ + m - 1 + hp * i)
                        r2 = n2_tmp[m % 2][:].rearrange("p (h t) -> p h t", h=2)
                        out = pair_of(t0 + m)
                        f(r2[:, 0], out[:, 0], ACT.Relu).then_inc(evac_a, 1)
                        f(r2[:, 1], out[:, 1], ACT.Relu).then_inc(evac_b, 1)

                    def high(m):
                        act.wait_ge(sq_in, h0_ + m + 1 + hp * i)
                        f(hid_hi[:, slot, m], n2_tmp[2 + m % 2][:], ACT.Copy).then_inc(hid_h, 1)

                    relu(0)
                    for m in range(1, 4):
                        relu(m)
                        high(m - 1)
                    high(3)
                if not (c0 + j + 2 >= CHUNKS and step == 0):
                    high_part(act, c0 + j + 2, i, step)

        def down(c0, i=0, step=0):
            for j in range(4):
                if not (c0 + j + 2 >= CHUNKS and step == 0):
                    high_part(act, c0 + j + 2, i, step)

        up(C_MLP, T_MLP, 0, 0)
        with act.Fori(0, FF_CHUNKS // 2 - 1) as i:
            up(C_MLP + 4, T_MLP + 4, 4, 1, i, 16)
            down(C_MLP + 8, i, 16)
            up(C_MLP + 12, T_MLP + 24, 8, 0, i, 16)
            down(C_MLP + 16, i, 16)
        up(CHUNKS - 12, T_LAST - 20, 60, 1)
        down(CHUNKS - 8)
        down(CHUNKS - 4)

    @block.vector
    def _(dve):
        own = Own(dve, dve_own)
        v = nc.vector

        dve.sem_inc(evac_b, 4)
        dve.wait_ge(consts_in, 32)

        def first_parts():
            low_part(dve, 0)
            low_part(dve, 1)

        norm_dve(dve, lambda t: x_in[:, t], lambda t: pcol("norm1", t), NORM1, n1_tmp, 0, 0, first_parts)
        dve.wait_ge(strips, 4)
        v.tensor_copy(logit[:, HALF:], bank[0:HEADS, 1, 0:HALF]).then_inc(evac_b, 1)
        low_part(dve, 2)
        with dve.Fori(0, IN_GROUPS) as g:
            for j in range(4):
                if j == 3:
                    for m in range(4):
                        dve.wait_ge(strips, 4 * (C_IN + 3) + m + 1 + 16 * g)
                        v.tensor_copy(proj[:, bass.ds(g, 1), m, HALF:].rearrange("p a t -> p (a t)"), pair_of(1 + m)[:, 1]
                                      ).then_inc(evac_b, 1)
                low_part(dve, C_IN + j + 2, g, 4)
        dve.wait_ge(evac_b, 4 + T_OUT)
        dve.wait_ge(w_low, C_OUT + 2)
        end_stage(dve, 1)

        PRE = CONV_W - 1
        dve.wait_ge(small_in, 16 * 5)
        v.tensor_copy(ext_conv[:, :, :, PRE:], proj[:, X_LRU, :, SEQ:].rearrange("p g (b t) -> p g b t", b=DEC_BATCH)
                      ).then_inc(ext_ready, 1)
        own.then(v.tensor_scalar(derived[:, 0:8], par[:, PARAM["ba"]:PARAM["ba"] + 8], -1.0, None, ALU.mult))
        own.then(v.tensor_scalar(derived[:, 20:21], pcol("fox_q"), HEAD_DIM ** -0.5, None, ALU.mult))
        own.then(v.tensor_scalar(derived[:, 8:12], par[:, PARAM["lam"]:PARAM["lam"] + 4], -1.0, 0.0, ALU.mult, ALU.max))
        own.wait()
        dve.wait_ge(lam_ln, 1)
        own.then(v.tensor_tensor(derived[:, 8:12], derived[:, 8:12], derived[:, 16:20], ALU.add))
        own.wait()
        own.then(v.tensor_scalar(derived[:, 12:16], derived[:, 8:12], LRU_C, None, ALU.mult))
        own.wait()
        v.tensor_scalar(derived[:, 8:12], derived[:, 8:12], -LRU_C, None, ALU.mult).then_inc(vecs_ready, 1)
        dve.wait_ge(ext_ready, 2)
        for g in range(GT):
            x = proj[:, X_LRU, g]
            y, ys = lx[:, g, 0:SEQ], lx[:, g, SEQ:].rearrange("p (b t) -> p b t", b=DEC_BATCH)

            def tap(k):
                return par[:, PARAM["conv_w"] + 4 * k + g:PARAM["conv_w"] + 4 * k + g + 1]

            own.then(v.tensor_scalar(y, x[:, 0:SEQ], tap(PRE), pcol("conv_b", g), ALU.mult, ALU.add))
            own.then(v.tensor_scalar(ys, ext_conv[:, g, :, PRE:], tap(PRE), pcol("conv_b", g), ALU.mult, ALU.add))
            for back in range(1, CONV_W):
                own.wait()
                a = v.scalar_tensor_tensor(out=y[:, back:], in0=x[:, 0:SEQ - back], scalar=tap(PRE - back),
                                           in1=y[:, back:], op0=ALU.mult, op1=ALU.add)
                b = v.scalar_tensor_tensor(out=ys, in0=ext_conv[:, g, :, PRE - back:PRE + DEC_SEQ - back],
                                           scalar=tap(PRE - back), in1=ys, op0=ALU.mult, op1=ALU.add)
                if back < PRE:
                    own.then(a)
                    own.then(b)
                else:
                    a.then_inc(conv_ready, 1)
                    b.then_inc(conv_ready, 1)
        dve.wait_ge(gate_read, 8)
        for e in (lr, li):
            own.then(v.tensor_scalar(e[:], e[:], 1.0, None, ALU.add))
            own.wait()
            ins = v.reciprocal(e[:], e[:])
            if e is lr:
                own.then(ins)
        ins.then_inc(gates_sig, 1)
        dve.wait_ge(gates_sig, 1)
        dve.wait_ge(conv_ready, 2 * GT)
        own.then(v.tensor_tensor(li[:], li[:], lx[:], ALU.mult))
        dve.wait_ge(decay_act, 8)
        own.then(v.tensor_tensor(lr[:], la[:], la[:], ALU.mult))
        own.wait()
        v.scalar_tensor_tensor(out=lm[:], in0=lr[:], scalar=1.0, in1=lm[:], op0=ALU.add, op1=ALU.mult
                               ).then_inc(mult_sq, 1)
        dve.wait_ge(mult_ready, 1)
        own.then(v.memset(lm[:, :, 0:1], 1.0))
        own.then(v.memset(seq_a[:], 0.0))
        own.wait()
        v.tensor_tensor(lm[:], lm[:], li[:], ALU.mult).then_inc(gelu_arg, 1)
        dve.wait_ge(gelu_arg, 1)

        def by_seq(t):
            return t[:, :, SEQ:].rearrange("p g (b t) -> p g b t", b=DEC_BATCH)

        own.then(v.tensor_copy(seq_a[:, :, :, 1:], by_seq(la)))
        own.then(v.tensor_copy(seq_u[:, :, :, 1:], by_seq(lm)))
        own.then(v.tensor_copy(seq_u[:, :, :, 0:1].rearrange("p g b t -> p g (b t)"), h0[:]))
        for g in range(GT):
            own.then(v.tensor_tensor_scan(lx[:, g, 0:SEQ], la[:, g, 0:SEQ], lm[:, g, 0:SEQ], 0.0, ALU.mult, ALU.add))
        own.wait()

        def row(t):
            return t[:].rearrange("p g b t -> p (g b t)")

        own.then(v.tensor_tensor_scan(row(seq_h), row(seq_a), row(seq_u), 0.0, ALU.mult, ALU.add))
        own.wait()
        own.then(v.tensor_copy(by_seq(lx), seq_h[:, :, :, 1:]))
        v.tensor_copy(last_h[:], lx[:, :, SEQ - 1:SEQ].rearrange("p g t -> p (g t)")).then_inc(lru_states, 1)
        v.tensor_copy(seq_last[:], seq_h[:, :, :, DEC_SEQ:].rearrange("p g b t -> p g (b t)")).then_inc(lru_states, 1)
        gate = proj[:, G_LRU]
        dve.wait_ge(gelu_in, 1)
        own.then(v.tensor_scalar(li[:], li[:], 0.044715, 1.0, ALU.mult, ALU.add))
        own.wait()
        v.tensor_tensor(li[:], li[:], gate, ALU.mult).then_inc(gelu_arg, 1)
        dve.wait_ge(gelu_tanh, 1)
        own.then(v.scalar_tensor_tensor(out=li[:], in0=li[:], scalar=1.0, in1=gate, op0=ALU.add, op1=ALU.mult))
        own.wait()
        dve.wait_ge(src_out, 32)
        own.then(v.scalar_tensor_tensor(out=proj[:, Y_LRU], in0=li[:], scalar=0.5, in1=lx[:], op0=ALU.mult, op1=ALU.mult))
        own.wait()
        dve.wait_ge(lru_states, 2)
        end_stage(dve, 2)

        own.then(v.tensor_scalar(sq_tmp[1][0:HEADS], logit[:], par[0:HEADS, PARAM["fox_b"]:PARAM["fox_b"] + 1], 0.0,
                                 ALU.add, ALU.min))
        own.wait()
        dve.wait_ge(lf_ln, 1)
        v.tensor_tensor(logit[:], sq_tmp[1][0:HEADS], rs_tmp[0][0:HEADS], ALU.subtract).then_inc(new_lf, 1)
        dve.wait_ge(new_lf, 1)
        v.tensor_tensor_scan(c_prompt[:], ones[0:HEADS, 0:1].to_broadcast([HEADS, SEQ]), logit[:, 0:SEQ], 0.0,
                             ALU.mult, ALU.add).then_inc(c_ready, 1)
        v.tensor_scalar(proj[:, SQ], proj[:, SQ], HEAD_DIM ** -0.5, None, ALU.mult).then_inc(q_scaled, 1)
        for t in range(8):
            x = proj[:, (FQ, FK)[t // 4], t % 4]
            dve.wait_ge(head_rs, t + 1)
            gain = derived[:, 20:21] if t < 4 else pcol("fox_k")
            v.scalar_tensor_tensor(out=x, in0=x, scalar=gain, in1=rs_tmp[t % 2][:], op0=ALU.mult, op1=ALU.mult
                                   ).then_inc(head_norm, 1)
        dve.wait_ge(head_norm, 8)
        dve.wait_ge(q_scaled, 1)
        dve.wait_ge(q_cleared, 1)
        for x in range(2):
            for h in range(2):
                o = HEAD_DIM * h
                src = proj[o:o + HEAD_DIM, (FQ, SQ)[x], :, SEQ:].rearrange("p h (b t) -> p b h t", b=DEC_BATCH)
                own.then(v.tensor_copy(q_pad[x][o:o + HEAD_DIM, :, :, DEC_SEQ * h:DEC_SEQ * h + DEC_SEQ], src))
            own.then(v.tensor_copy(k_new[x][:], proj[:, (FK, SK)[x], :, SEQ:]))

        for i in range(UNITS + 4):
            if i < UNITS:
                n = (i % 4 + 1) * P
                dve.wait_ge(f_score, i + 1)
                v.tensor_reduce(stat[:, i % 3, 0:1], bank[:, i % 2, 0:n], AX_X, ALU.max, negate=True).then_inc(f_max, 1)
            if 2 <= i < UNITS + 2:
                k = i - 2
                n = (k % 4 + 1) * P
                dve.wait_ge(f_pt, k + 1)
                if k >= 2:
                    dve.wait_ge(f_av, k - 1)
                v.tensor_copy(ptf[k % 2][:, 0:n], bank[:, 4, 0:n]).then_inc(f_ptsb, 1)
            if 1 <= i <= UNITS:
                k = i - 1
                n = (k % 4 + 1) * P
                dve.wait_ge(f_exp, k + 1)
                own.then(v.reciprocal(stat[:, k % 3, 2:3], stat[:, k % 3, 1:2]))
                own.wait()
                v.tensor_scalar(pf[k % 3][:, 0:n], pf[k % 3][:, 0:n], stat[:, k % 3, 2:3], None, ALU.mult
                                ).then_inc(f_prob, 1)
                a, c, z = pa[k % 2][:, 0:n], pc[k % 2][:, 0:n], bank[:, 2 + k % 2, 0:n]
                dve.wait_ge(s_ln, k + 1)
                own.then(v.scalar_tensor_tensor(out=a, in0=z, scalar=0.0, in1=a, op0=ALU.max, op1=ALU.add))
                own.wait()
                own.then(v.tensor_tensor_scan(c[:, ::-1], ones[:, 0:1].to_broadcast([P, n]), a[:, ::-1], 0.0,
                                              ALU.mult, ALU.add))
                own.wait()
                v.tensor_tensor(a, z, c, ALU.subtract).then_inc(s_diff, 1)
            if 3 <= i < UNITS + 3:
                k = i - 3
                n = (k % 4 + 1) * P
                dve.wait_ge(s_pt, k + 1)
                if k >= 2:
                    dve.wait_ge(s_av, k - 1)
                v.tensor_copy(pts[k % 2][:, 0:n], bank[:, 5, 0:n]).then_inc(s_ptsb, 1)
                h, q = divmod(k, 4)
                o = HEAD_DIM * (h % 2)
                dve.wait_ge(f_av, k + 1)
                v.tensor_copy(proj[o:o + HEAD_DIM, Y_FOX, h // 2, P * q:P * q + P], bank[o:o + HEAD_DIM, 6, 0:P]
                              ).then_inc(f_y, 1)
        dve.wait_ge(f_y, UNITS)
        own.wait()
        end_stage(dve, 3)

        n_rows = DEC_BATCH * HEADS
        v.tensor_tensor_scan(log_decay[:], ones[0:n_rows, 0:1].to_broadcast([n_rows, KEYS]), log_decay[:], 0.0,
                             ALU.mult, ALU.add).then_inc(ld_ready, 1)

        def copy_scores(b, x, first=False):
            dst = (s_fox, s_z)[x]
            if not first:
                dve.wait_ge(d_pt, 10 * b + 5 * x - 5)
            for blk in range(5):
                dve.wait_ge(d_score, 10 * b + 5 * x + blk + 1)
                n = 512 if blk < 4 else NEW
                v.tensor_copy(dst[:, 512 * blk:512 * blk + n], bank[:, blk, 0:n]).then_inc(d_copied, 1)
            dve.wait_ge(d_copied, 10 * b + 5 * x + 5)

        def fox_max(b):
            v.tensor_reduce(dstat[:, 0:1], s_fox[:], AX_X, ALU.max, negate=True).then_inc(d_max, 1)

        def sb_sums(b):
            dve.wait_ge(d_ln, b + 1)
            v.scalar_tensor_tensor(out=s_l[:], in0=s_z[:], scalar=0.0, in1=s_l[:], op0=ALU.max, op1=ALU.add
                                   ).then_inc(d_sp, 1)
            dve.wait_ge(d_sp, b + 1)
            v.tensor_tensor_scan(s_r[:, ::-1], ones[:, 0:1].to_broadcast([P, KEYS]), s_l[:, ::-1], 0.0,
                                 ALU.mult, ALU.add).then_inc(d_sum, 1)
            dve.wait_ge(d_sum, b + 1)
            v.tensor_tensor(s_z[:], s_z[:], s_r[:], ALU.subtract).then_inc(d_diff, 1)

        def out_rows(b, x, first=False):
            u = 2 * b + x
            if x == 0:
                dve.wait_ge(d_exp, b + 1)
                v.reciprocal(dstat[:, 2:3], dstat[:, 1:2]).then_inc(d_rinv, 1)
                dve.wait_ge(d_rinv, b + 1)
            dve.wait_ge(d_av, 5 * u + 5)
            if not first:
                dve.wait_ge(d_ot, u)
            if x == 0:
                v.tensor_scalar(o_sb[:], bank[:, 7, 0:P], dstat[:, 2:3], None, ALU.mult).then_inc(d_o, 1)
            else:
                v.tensor_copy(o_sb[:], bank[:, 7, 0:P]).then_inc(d_o, 1)

        def out_features(b, x):
            dve.wait_ge(d_ot, 2 * b + x + 1)
            turned = bank[:, 7, P:2 * P].rearrange("p (a r) -> p a r", a=PAIRS)
            for h in range(2):
                o = HEAD_DIM * h
                v.tensor_copy(proj[o:o + HEAD_DIM, (Y_FOX, Y_SB)[x], :, bass.ds(SEQ + DEC_SEQ * b, DEC_SEQ)],
                              turned[o:o + HEAD_DIM, :, DEC_SEQ * h:DEC_SEQ * h + DEC_SEQ]).then_inc(d_y, 1)

        copy_scores(0, 0, True)
        fox_max(0)
        copy_scores(0, 1, True)
        sb_sums(0)
        out_rows(0, 0, True)
        with dve.Fori(1, DEC_BATCH) as b:
            copy_scores(b, 0)
            fox_max(b)
            out_features(b - 1, 0)
            out_rows(b - 1, 1)
            copy_scores(b, 1)
            out_features(b - 1, 1)
            sb_sums(b)
            out_rows(b, 0)
        out_features(DEC_BATCH - 1, 0)
        out_rows(DEC_BATCH - 1, 1)
        out_features(DEC_BATCH - 1, 1)
        dve.wait_ge(d_y, 4 * DEC_BATCH)
        end_stage(dve, 4)

        for c in (C_OUT, C_OUT + 1):
            dve.wait_ge(again_high, c - C_OUT + 1)
            v.tensor_tensor(w_lo[c % 2][:], w_raw[c % 2][:], w_hi[c % 2][:].bitcast(F32), ALU.subtract
                            ).then_inc(again_low, 1)
        norm_dve(dve, y_src, lambda t: pcol("out_g", t), NORMY, n2_tmp, KT, 1)

        def add_to_x(c0, t0, first_tile, i=0, step=0):
            for m in range(4):
                n = t0 + m
                x = x_res[:, first_tile + m]
                dve.wait_ge(strips, 4 * c0 + m + 1 + 4 * step * i)
                dve.wait_ge(evac_b, n + 1 + step * 40 // 16 * i)
                for h, free in enumerate((evac_a, evac_b)):
                    t = slice(h * HALF, h * HALF + HALF)
                    v.tensor_tensor(x[:, t], x[:, t], pair_of(n)[:, h], ALU.add).then_inc(free, 1)

        dve.wait_ge(xr_in, 64)
        for g in range(OUT_GROUPS):
            c = C_OUT + 4 * g
            for j in range(4):
                if j == 3:
                    add_to_x(c + 3, T_OUT + 4 * g, 4 * g)
                low_part(dve, c + j + 2)
            sum_tiles(dve, 0, range(4 * g, 4 * g + 4), n2_tmp, 2 * KT)
        norm_dve(dve, lambda t: x_res[:, t], lambda t: pcol("norm2", t), NORM2, n2_tmp, 2 * KT, 5, summed_up=True)

        def up(c0, t0, h0_, slot, i=0, step=0):
            hp, per = step // 2, step * 40 // 16
            for j in range(4):
                if j == 3:
                    def square(m):
                        dve.wait_ge(evac_b, 4 + t0 + m + 1 + per * i)
                        if not (h0_ + m < 2 and step == 0):
                            dve.wait_ge(hid_l, h0_ + m - 1 + hp * i)
                        v.tensor_tensor(n2_tmp[2 + m % 2][:], n2_tmp[m % 2][:], n2_tmp[m % 2][:], ALU.mult
                                        ).then_inc(sq_in, 1)

                    def low(m):
                        dve.wait_ge(hid_h, h0_ + m + 1 + hp * i)
                        v.tensor_tensor(hid_lo[:, slot, m], n2_tmp[2 + m % 2][:], hid_hi[:, slot, m].bitcast(F32),
                                        ALU.subtract).then_inc(hid_l, 1)

                    square(0)
                    for m in range(1, 4):
                        square(m)
                        low(m - 1)
                    low(3)
                if not (c0 + j + 2 >= CHUNKS and step == 0):
                    low_part(dve, c0 + j + 2, i, step)

        def down(c0, t0, i=0, step=0):
            for j in range(4):
                add_to_x(c0 + j, t0 + 4 * j, 4 * j, i, step)
                if not (c0 + j + 2 >= CHUNKS and step == 0):
                    low_part(dve, c0 + j + 2, i, step)

        up(C_MLP, T_MLP, 0, 0)
        with dve.Fori(0, FF_CHUNKS // 2 - 1) as i:
            up(C_MLP + 4, T_MLP + 4, 4, 1, i, 16)
            down(C_MLP + 8, T_MLP + 8, i, 16)
            up(C_MLP + 12, T_MLP + 24, 8, 0, i, 16)
            down(C_MLP + 16, T_MLP + 28, i, 16)
        up(CHUNKS - 12, T_LAST - 20, 60, 1)
        down(CHUNKS - 8, T_LAST - 16)
        down(CHUNKS - 4, T_LAST)

    @block.tensor
    def _(pe):
        mm = nc.tensor.matmul

        pe.wait_ge(consts_in, 32)
        norm_pe(pe, NORM1, n1_tmp, 0, 0)
        pe.wait_ge(w_low, 1)
        hi = w_hi[0][:].rearrange("p (k n) -> p k n", k=KT)
        lo = w_lo[0][:].rearrange("p (k n) -> p k n", k=KT)
        for k in range(KT):
            pe.wait_ge(a_low, k + 1)
            for w, a in ((hi, act_hi), (hi, act_lo), (lo, act_hi)):
                for h in range(2):
                    last = k == KT - 1 and w is lo
                    ins = mm(bank[:, h, 0:HALF], w[:, k], a[:, k, h * HALF:h * HALF + HALF],
                             start=(k == 0 and w is hi and a is act_hi), stop=last)
            if k % 4 == 3:
                ins.then_inc(strips, 1)
        with pe.Fori(0, IN_GROUPS) as g:
            for j in range(4):
                multiply(pe, C_IN + j, act_hi[:, 4 * j:4 * j + 4], act_lo[:, 4 * j:4 * j + 4], j == 0, j == 3,
                         g, 4, (1, 4))
        pe.wait_ge(strips, 4 * C_OUT)
        end_stage(pe, 1)

        pe.wait_ge(small_in, 16 * 5)
        for n in range(12):
            g = n % 4
            if n >= 4:
                pe.wait_ge(gate_read, n - 3)
            if n < 8:
                pe.wait_ge(conv_ready, 2 * (g + 1))
                w, x = lru_w_sb[:, n // 4, g], lx[:, g]
            else:
                pe.wait_ge(pool_diff, g + 1)
                w, x = pool_w_sb[:, g], pool_d[g % 2][:]
            for h in range(2):
                ins = mm(pair_of(n)[:, h], w, x[:, h * HALF:h * HALF + HALF], start=True, stop=True)
            ins.then_inc(gate_mm, 1)
        pe.wait_ge(gate_mm, 12)
        end_stage(pe, 2)

        def turn_values(n):
            x, tt = divmod(n, 5)
            if n >= 4:
                pe.wait_ge(v_stored, n - 3)
            rows = P if tt < 4 else NEW
            for ft in range(GT):
                ins = nc.tensor.transpose(bank[0:rows, 4 + n % 4, P * ft:P * ft + P],
                                          proj[:, (FV, SV)[x], ft, P * tt:P * tt + rows], ident)
            ins.then_inc(v_turned, 1)

        for t in range(8):
            turn_values(t)
            pe.wait_ge(head_sq, t + 1)
            if t >= 2:
                pe.wait_ge(head_rs, t - 1)
            for h in range(2):
                ins = mm(bank[:, 2 * (t % 2) + h, 0:HALF], same_head, sq_tmp[t % 2][:, h * HALF:h * HALF + HALF],
                         start=True, stop=True)
            ins.then_inc(head_sum, 1)
        turn_values(8)
        turn_values(9)

        pe.wait_ge(head_norm, 8)
        pe.wait_ge(q_scaled, 1)
        pe.wait_ge(c_ready, 1)
        pe.wait_ge(signs_in, 32)
        pe.wait_ge(v_stored, 10)

        def scores(i, x):
            h, q = divmod(i, 4)
            o, n = HEAD_DIM * (h % 2), P * (q + 1)
            s = bank[:, 2 * x + i % 2, 0:n]
            if x == 0:
                mm(s, neg_head_sb[:, P * h:P * h + P], c_prompt[:, 0:n], start=True, stop=False)
            mm(s, proj[o:o + HEAD_DIM, (FQ, SQ)[x], h // 2, P * q:P * q + P],
               proj[o:o + HEAD_DIM, (FK, SK)[x], h // 2, 0:n], start=(x == 1), stop=False)
            mm(s[:, P * q:n], ident, cc(("fox_mask", "sb_mask")[x], 0, P), start=False, stop=True
               ).then_inc((f_score, s_score)[x], 1)

        def turn(k, x):
            src, n = (pf[k % 3], ps[k % 2])[x], k % 4 + 1
            for j in range(n):
                ins = nc.tensor.transpose(bank[:, 4 + x, P * j:P * j + P], src[:, P * j:P * j + P], ident)
            ins.then_inc((f_pt, s_pt)[x], 1)

        def weigh(k, x):
            h, q = divmod(k, 4)
            o = HEAD_DIM * (h % 2)
            src = (ptf, pts)[x][k % 2]
            for j in range(q + 1):
                ins = mm(bank[o:o + HEAD_DIM, 6 + x, 0:P], v_tok[x][:, j, HEAD_DIM * h:HEAD_DIM * h + HEAD_DIM],
                         src[:, P * j:P * j + P], start=(j == 0), stop=(j == q))
            ins.then_inc((f_av, s_av)[x], 1)

        for i in range(UNITS + 4):
            if i < UNITS:
                if i >= 2:
                    pe.wait_ge(f_exp, i - 1)
                scores(i, 0)
                if i >= 2:
                    pe.wait_ge(s_diff, i - 1)
                scores(i, 1)
            if 2 <= i < UNITS + 2:
                k = i - 2
                pe.wait_ge(f_prob, k + 1)
                if k >= 1:
                    pe.wait_ge(f_ptsb, k)
                turn(k, 0)
            if 3 <= i < UNITS + 3:
                k = i - 3
                pe.wait_ge(f_ptsb, k + 1)
                if k >= 1:
                    pe.wait_ge(f_y, k)
                weigh(k, 0)
                pe.wait_ge(s_prob, k + 1)
                if k >= 1:
                    pe.wait_ge(s_ptsb, k)
                turn(k, 1)
            if i >= 4:
                k = i - 4
                pe.wait_ge(s_ptsb, k + 1)
                if k >= 1:
                    pe.wait_ge(s_y, k)
                weigh(k, 1)
        pe.wait_ge(s_av, UNITS)
        end_stage(pe, 3)

        def seq_scores(b, x, first=False):
            u = 2 * b + x
            if x == 0:
                pe.wait_ge(q_staged, 2 * b + 2)
            else:
                pe.wait_ge(s_staged, b + 1)
            for blk in range(5):
                n = 512 if blk < 4 else NEW
                if blk < 4:
                    pe.wait_ge(k_loaded[blk], 64 * (u + 1))
                if not first:
                    pe.wait_ge(d_copied, 5 * u + blk - 4)
                s = bank[:, blk, 0:n]
                if x == 0:
                    mm(s, neg_now[:], log_decay[:, 512 * blk:512 * blk + n], start=True, stop=False)
                for a in range(PAIRS):
                    rhs = k_ring[:, blk, :, a] if blk < 4 else k_new[x][:, a]
                    ins = mm(bank[ROWS * a:ROWS * a + ROWS, blk, 0:n], q_now[x][:, a], rhs, start=(x == 1),
                             stop=(blk < 4))
                if blk == 4:
                    masks = cc(("fox_new", "sb_new")[x], 0, DEC_BATCH * NEW)
                    ins = mm(s, ident, masks[:, bass.ds(NEW * b, NEW)], start=False, stop=True)
                ins.then_inc(d_score, 1)

        def seq_turn(b, x, g, first):
            G = 10 * b + 5 * x + g
            if g >= 2:
                pe.wait_ge(d_ptsb, G - 1)
            elif not first:
                pe.wait_ge(d_ptsb, G - 2 * g)
            src = (s_fox, s_z)[x]
            if g < 4:
                for j in range(4):
                    c = PAGE * (4 * g + j)
                    ins = nc.tensor.transpose(bank[:, 5 + g % 2, P * j:P * j + P], src[:, c:c + PAGE], ident)
            else:
                ins = nc.tensor.transpose(bank[0:NEW, 5, 0:P], src[:, PAST:KEYS], ident)
            ins.then_inc(d_pt, 1)

        def seq_weigh(b, x, g, first):
            u = 2 * b + x
            if g < 4:
                pe.wait_ge(d_ptsb, 5 * u + g + (1 if g < 3 else 2))
                pe.wait_ge(v_loaded[x][g], 64 * (b + 1))
            if g == 0 and not first:
                pe.wait_ge(d_y, 2 * u)
            for j in range(4 if g < 4 else 1):
                for a in range(PAIRS):
                    rows, cols = slice(ROWS * a, ROWS * a + ROWS), slice(P * a, P * a + P)
                    if g < 4:
                        w, vals = p_t[:, g % 2, j, rows], v_ring[x][:, 4 * g + j, cols]
                    else:
                        w, vals = p_t[0:NEW, 0, 0, rows], v_new[x][:, cols]
                    ins = mm(bank[rows, 7, 0:P], w, vals, start=(g == 0 and j == 0), stop=(g == 4))
            ins.then_inc(d_av, 1)

        def seq_output(b, x, first=False):
            pe.wait_ge(*((d_exp, b + 1) if x == 0 else (d_wgt, b + 1)))
            seq_turn(b, x, 0, first)
            for g in range(1, 5):
                seq_turn(b, x, g, first)
                seq_weigh(b, x, g - 1, first)
            seq_weigh(b, x, 4, first)

        def turn_output(b, x):
            pe.wait_ge(d_o, 2 * b + x + 1)
            nc.tensor.transpose(bank[:, 7, P:2 * P], o_sb[:], ident).then_inc(d_ot, 1)

        pe.wait_ge(ld_ready, 1)
        seq_scores(0, 0, True)
        seq_scores(0, 1)
        seq_output(0, 0, True)
        with pe.Fori(1, DEC_BATCH) as b:
            seq_scores(b, 0)
            turn_output(b - 1, 0)
            seq_output(b - 1, 1)
            seq_scores(b, 1)
            turn_output(b - 1, 1)
            seq_output(b, 0)
        turn_output(DEC_BATCH - 1, 0)
        seq_output(DEC_BATCH - 1, 1)
        turn_output(DEC_BATCH - 1, 1)
        pe.wait_ge(d_ot, 2 * DEC_BATCH)
        end_stage(pe, 4)

        pe.wait_ge(again_low, 2)
        norm_pe(pe, NORMY, n2_tmp, KT, 1)
        pe.wait_ge(rstd, 5)
        for g in range(OUT_GROUPS):
            for j in range(4):
                multiply(pe, C_OUT + 4 * g + j, act_hi[:, 4 * j:4 * j + 4], act_lo[:, 4 * j:4 * j + 4], j == 0, j == 3,
                         tile0=(T_OUT + 4 * g, 0), split=KT + 4 * (j + 1))
        norm_pe(pe, NORM2, n2_tmp, 2 * KT, 5)
        pe.wait_ge(rstd, 6)

        def up(c0, t0, i=0, step=0):
            for j in range(4):
                multiply(pe, c0 + j, act_hi[:, 4 * j:4 * j + 4], act_lo[:, 4 * j:4 * j + 4], j == 0, j == 3,
                         i, step, (t0, step * 40 // 16), split=2 * KT + 4 * (j + 1))

        def down(c0, t0, h0_, slot, i=0, step=0):
            pe.wait_ge(hid_l, h0_ + 4 + step // 2 * i)
            for j in range(4):
                multiply(pe, c0 + j, hid_hi[:, slot], hid_lo[:, slot], True, True, i, step,
                         (t0 + 4 * j, step * 40 // 16))

        up(C_MLP, T_MLP)
        with pe.Fori(0, FF_CHUNKS // 2 - 1) as i:
            up(C_MLP + 4, T_MLP + 4, i, 16)
            down(C_MLP + 8, T_MLP + 8, 0, 0, i, 16)
            up(C_MLP + 12, T_MLP + 24, i, 16)
            down(C_MLP + 16, T_MLP + 28, 4, 1, i, 16)
        up(CHUNKS - 12, T_LAST - 20)
        down(CHUNKS - 8, T_LAST - 16, 56, 0)
        down(CHUNKS - 4, T_LAST, 60, 1)

    ctx.close()


def constants():
    c = np.zeros((P, N_CONST), np.float32)

    def put(name, a):
        c[:, CONST[name]:CONST[name] + a.shape[1]] = a

    i, j = np.indices((P, P))
    put("ident", (i == j).astype(np.float32))
    put("ones", np.ones((P, P), np.float32))
    put("same_head", (i // HEAD_DIM == j // HEAD_DIM).astype(np.float32))
    put("fox_mask", np.where(j <= i, 0, MASKED).astype(np.float32))
    put("sb_mask", np.where(j < i, 0, MASKED).astype(np.float32))
    row, b, k = np.indices((P, DEC_BATCH, NEW))
    query = row % DEC_SEQ
    mine = k // DEC_SEQ == b
    put("fox_new", np.where(mine & (k % DEC_SEQ <= query), 0, MASKED).astype(np.float32).reshape(P, -1))
    put("sb_new", np.where(mine & (k % DEC_SEQ < query), 0, MASKED).astype(np.float32).reshape(P, -1))
    _, g, t = np.indices((P, GT, POOL_MAX))
    put("pool_rec", (1.0 / np.minimum(2 ** (g + 1), t + 1)).astype(np.float32).reshape(P, -1))
    h, c_ = np.indices((HEADS, HEADS * P))
    neg_head = np.where(c_ // P == h, -1, 0).astype(np.float32)
    s, c_ = np.indices((DEC_BATCH * HEADS, DEC_BATCH * P))
    b, r = c_ // P, c_ % P
    head = 2 * (r // ROWS) + (r % ROWS) // DEC_SEQ
    neg_seq = np.where((r % ROWS < 2 * DEC_SEQ) & (s == HEADS * b + head), -1, 0).astype(np.float32)
    return c, neg_head, neg_seq


def kernel(**inputs):
    from concourse import bacc
    from concourse.bass_utils import run_bass_kernel_spmd

    a = {k: np.asarray(v) for k, v in inputs.items()}

    def feature_major(x, lead):
        x = np.moveaxis(x, -1, 0)
        return np.ascontiguousarray(np.swapaxes(x.reshape((-1, P) + x.shape[1:]), 0, 1))

    x = np.concatenate([a["x_prompt"].reshape(SEQ, D_MODEL), a["x_sample"].reshape(NEW, D_MODEL)])

    def tiles(w, n):
        r, c = w.shape
        return w.reshape(r // 512, 4, P, c // n, n).transpose(3, 0, 2, 1, 4).reshape(c // n, r // 512, P, 4 * n)

    w_in = a["w_in"][0]
    n_log = 6 * D_GROUP
    logits = w_in[:, n_log:n_log + P].reshape(KT, P, P).transpose(1, 0, 2).reshape(1, P, CHUNK)
    heads = np.concatenate([w_in[:, :n_log], w_in[:, n_log + HEADS:]], axis=1)
    up = tiles(a["w_up"][0], 512)
    down = tiles(a["w_down"][0], 512).transpose(1, 0, 2, 3)
    mlp = [up[0]]
    for f in range(FF_CHUNKS - 1):
        mlp += [up[f + 1], down[f]]
    mlp.append(down[FF_CHUNKS - 1])
    weights = np.concatenate([logits, tiles(heads, 512).reshape(-1, P, CHUNK),
                              tiles(a["w_out"][0], 512).reshape(-1, P, CHUNK)] + mlp)

    def cols(v):
        return v.reshape(-1, P).T

    pad = np.zeros((P, 1), np.float32)
    pad[:HEADS, 0] = a["fox_bf"][0]
    head_row = (np.arange(P) % HEADS).astype(np.float32)[:, None]
    params = np.concatenate([
        cols(a["norm1_g"][0]), cols(a["norm2_g"][0]), cols(a["out_g"][0]), cols(a["pool_scale"][0]),
        cols(a["conv_w"][0]), cols(a["conv_b"][0]), cols(a["lru_ba"][0]), cols(a["lru_bx"][0]),
        cols(a["lru_lambda"][0]), np.tile(a["fox_q_g"][0], 2)[:, None], np.tile(a["fox_k_g"][0], 2)[:, None],
        pad, head_row], axis=1)
    assert params.shape == (P, N_PARAM)

    def block_diagonal(w):
        out = np.zeros((P, GT, P), np.float32)
        for n in range(8):
            o = 64 * (n % 2)
            out[o:o + 64, n // 2, o:o + 64] = w[n]
        return out

    def cache(c):
        c = c[0]
        k = c[:, :, 0].reshape(-1, PAGE, PAIRS, 2, HEAD_DIM).transpose(0, 3, 4, 2, 1).reshape(-1, P, PAIRS * PAGE)
        return np.ascontiguousarray(k), np.ascontiguousarray(c[:, :, 1].reshape(-1, PAGE, D_GROUP))

    fox_k, fox_v = cache(a["cache_fox_kv"])
    sb_k, sb_v = cache(a["cache_sb_kv"])
    consts, neg_head, neg_seq = constants()
    table = a["page_table"]
    arrays = {
        "xT": feature_major(x, 1), "weights": weights, "params": params, "consts": consts,
        "neg_head": neg_head, "neg_seq": neg_seq,
        "pool_w": a["pool_w"][0].transpose(1, 0, 2),
        "lru_w": np.stack([block_diagonal(a["lru_wa"][0]), block_diagonal(a["lru_wx"][0])], axis=1),
        "state_pool": feature_major(a["state_pool"][0], 2), "state_conv": feature_major(a["state_conv"][0], 2),
        "state_lru": feature_major(a["state_lru"][0], 1),
        "fox_k": fox_k, "fox_v": fox_v, "sb_k": sb_k, "sb_v": sb_v,
        "logf_cache": a["cache_fox_logf"][0].transpose(0, 2, 1).reshape(-1, PAGE),
        "page_rows": np.repeat(table, HEADS, axis=0), "page_ids": table.reshape(1, -1),
    }
    arrays = {k: np.ascontiguousarray(v) for k, v in arrays.items()}
    shapes = {
        "y_out": (P, KT, TOK), "kv_out": (4, P, GT, TOK), "logf_out": (HEADS, TOK),
        "pool_p": (P, GT, POOL_MAX - 1), "conv_p": (P, GT, CONV_W - 1), "lru_p": (P, GT),
        "pool_s": (P, GT, DEC_BATCH, POOL_MAX - 1), "conv_s": (P, GT, DEC_BATCH, CONV_W - 1),
        "lru_s": (P, GT, DEC_BATCH),
    }
    nc = bacc.Bacc("TRN2", target_bir_lowering=False, num_devices=1)
    args = {k: nc.dram_tensor(k, v.shape, mybir.dt.from_np(v.dtype), kind="ExternalInput").ap() for k, v in arrays.items()}
    args |= {k: nc.dram_tensor(k, s, F32, kind="ExternalOutput").ap() for k, s in shapes.items()}
    build_step(nc, **args)
    got = run_bass_kernel_spmd(nc, [arrays], core_ids=[0]).results[0]

    def tokens_major(y):
        y = np.swapaxes(y, 0, 1)
        return np.moveaxis(y.reshape((-1,) + y.shape[2:]), 0, -1)

    y = tokens_major(got["y_out"])
    kv = [tokens_major(got["kv_out"][i]).reshape(TOK, HEADS, HEAD_DIM) for i in range(4)]
    fox, sb = np.stack(kv[:2], axis=1), np.stack(kv[2:], axis=1)
    logf = got["logf_out"].T

    def new(v):
        return v[SEQ:].reshape((1, DEC_BATCH, DEC_SEQ) + v.shape[1:])

    return (y[:SEQ].reshape(1, SEQ, D_MODEL), y[SEQ:].reshape(DEC_BATCH, DEC_SEQ, D_MODEL),
            fox[None, None, :SEQ], logf[None, None, :SEQ], sb[None, None, :SEQ],
            tokens_major(got["pool_p"])[None, None], tokens_major(got["conv_p"])[None, None],
            tokens_major(got["lru_p"])[None, None],
            new(fox), new(logf), new(sb),
            tokens_major(got["pool_s"])[None], tokens_major(got["conv_s"])[None], tokens_major(got["lru_s"])[None])
```
